# Optimizing a Trainium2 kernel written in Bass

```python
import jax, jax.numpy as jnp
from jax import lax
import numpy as np

D_MODEL = 1024
BATCH = 1
SEQ = 2048
DEPTH = 2

CHUNK = 64
D_MIX = D_MODEL
HEAD_DIM = 64
ATT_WIDTH = D_MIX // 2
ATT_HEADS = ATT_WIDTH // HEAD_DIM
ATT_KV_HEADS = ATT_HEADS // 4
ATT_GROUP = ATT_HEADS // ATT_KV_HEADS
KV_WIDTH = ATT_KV_HEADS * HEAD_DIM
WINDOW = 128
WINDOW_CHUNKS = WINDOW // CHUNK
POOL_WIDTH = D_MIX // 4
POOL_WINDOWS = (2, 4, 8, 16)
POOL_GROUPS = len(POOL_WINDOWS)
POOL_GROUP_DIM = POOL_WIDTH // POOL_GROUPS
RET_WIDTH = D_MIX // 4
RET_HEADS = RET_WIDTH // HEAD_DIM
ROPE_BASE = 10000.0
IN_SIZES = (ATT_WIDTH, KV_WIDTH, KV_WIDTH, POOL_WIDTH, RET_WIDTH, RET_WIDTH, RET_WIDTH, RET_WIDTH)
D_IN = sum(IN_SIZES)
IN_SPLITS = [int(s) for s in np.cumsum(IN_SIZES)[:-1]]
N_EXPERTS = 32
N_EXPERT_GROUPS = 8
EXPERTS_PER_GROUP = N_EXPERTS // N_EXPERT_GROUPS
TOP_K = 2
D_EXPERT = D_MODEL // 2
EPS = 1e-6

kernel_name = "hybrid_swa_pool_retention_grouped_moe"

def rms_norm(x, g=None):
    xf = x.astype(jnp.float32)
    y = xf * lax.rsqrt(jnp.mean(xf * xf, axis=-1, keepdims=True) + EPS)
    if g is not None:
        y = y * g.astype(jnp.float32)
    return y.astype(x.dtype)

def rope(x, pos):
    half = x.shape[-1] // 2
    freq = 1.0 / (ROPE_BASE ** (jnp.arange(half, dtype=jnp.float32) / half))
    ang = pos[:, None] * freq[None, :]
    cos = jnp.cos(ang)[None, :, None, :]
    sin = jnp.sin(ang)[None, :, None, :]
    x1, x2 = x[..., :half], x[..., half:]
    return jnp.concatenate([x1 * cos - x2 * sin, x1 * sin + x2 * cos], axis=-1)

def _chunk_context(t):
    nc = t.shape[1]
    parts = []
    for j in range(WINDOW_CHUNKS - 1, -1, -1):
        if j == 0:
            parts.append(t)
        else:
            pad = [(0, 0), (j, 0)] + [(0, 0)] * (t.ndim - 2)
            parts.append(jnp.pad(t, pad)[:, :nc])
    return jnp.concatenate(parts, axis=2)

def sliding_window_sink_attention(q, k, v, q_gain, k_gain, sinks):
    b, s, _ = q.shape
    nc = s // CHUNK
    q = rms_norm(q.reshape(b, s, ATT_HEADS, HEAD_DIM), q_gain)
    k = rms_norm(k.reshape(b, s, ATT_KV_HEADS, HEAD_DIM), k_gain)
    v = v.reshape(b, s, ATT_KV_HEADS, HEAD_DIM)
    qb = q.reshape(b, nc, CHUNK, ATT_KV_HEADS, ATT_GROUP, HEAD_DIM)
    kb = _chunk_context(k.reshape(b, nc, CHUNK, ATT_KV_HEADS, HEAD_DIM))
    vb = _chunk_context(v.reshape(b, nc, CHUNK, ATT_KV_HEADS, HEAD_DIM))
    sc = jnp.einsum('bnqhgd,bnkhd->bnhgqk', qb, kb).astype(jnp.float32) * (HEAD_DIM ** -0.5)
    key_shift = WINDOW_CHUNKS - 1 - jnp.arange(WINDOW_CHUNKS * CHUNK) // CHUNK
    valid = jnp.arange(nc)[:, None] >= key_shift[None, :]
    sc = jnp.where(valid[None, :, None, None, None, :], sc, jnp.finfo(jnp.float32).min)
    sink = jnp.broadcast_to(sinks.astype(jnp.float32).reshape(1, 1, ATT_KV_HEADS, ATT_GROUP, 1, 1),
                            sc.shape[:-1] + (1,))
    p = jax.nn.softmax(jnp.concatenate([sc, sink], axis=-1), axis=-1)[..., :-1]
    o = jnp.einsum('bnhgqk,bnkhd->bnqhgd', p.astype(vb.dtype), vb)
    return o.reshape(b, s, ATT_WIDTH)

def multiscale_pool(u, pool_w, pool_scale):
    b, s, _ = u.shape
    uf = u.astype(jnp.float32)
    cs = jnp.cumsum(uf, axis=1)
    t1 = jnp.arange(1, s + 1, dtype=jnp.float32)[None, :, None]
    outs = []
    for gi, w in enumerate(POOL_WINDOWS):
        sl = slice(gi * POOL_GROUP_DIM, (gi + 1) * POOL_GROUP_DIM)
        c = cs[..., sl]
        shifted = jnp.pad(c, ((0, 0), (w, 0), (0, 0)))[:, :s]
        mean = (c - shifted) / jnp.minimum(t1, float(w))
        outs.append(mean - uf[..., sl])
    d = jnp.stack(outs, axis=2)
    y = jnp.einsum('bsgc,gce->bsge', d, pool_w.astype(jnp.float32)).reshape(b, s, POOL_WIDTH)
    return (y * pool_scale.astype(jnp.float32)).astype(u.dtype)

def retention(q, k, v, g, pos):
    b, s, _ = q.shape
    nc = s // CHUNK
    q = rope(q.astype(jnp.float32).reshape(b, s, RET_HEADS, HEAD_DIM), pos)
    k = rope(k.astype(jnp.float32).reshape(b, s, RET_HEADS, HEAD_DIM), pos) * (HEAD_DIM ** -0.5)
    v = v.astype(jnp.float32).reshape(b, s, RET_HEADS, HEAD_DIM)
    gamma = 1.0 - jnp.power(2.0, -5.0 - jnp.arange(RET_HEADS, dtype=jnp.float32))
    idx = jnp.arange(CHUNK, dtype=jnp.float32)
    diff = idx[:, None] - idx[None, :]
    dmask = jnp.where(diff >= 0, gamma[:, None, None] ** jnp.maximum(diff, 0.0), 0.0)
    qc = q.reshape(b, nc, CHUNK, RET_HEADS, HEAD_DIM)
    kc = k.reshape(b, nc, CHUNK, RET_HEADS, HEAD_DIM)
    vc = v.reshape(b, nc, CHUNK, RET_HEADS, HEAD_DIM)
    inner = jnp.einsum('bnqhd,bnkhd->bnhqk', qc, kc) * dmask
    inner = jnp.einsum('bnhqk,bnkhe->bnqhe', inner, vc)
    zeta = gamma[:, None] ** (CHUNK - 1.0 - idx)[None, :]
    xi = gamma[:, None] ** (idx + 1.0)[None, :]
    kv = jnp.einsum('bnkhd,hk,bnkhe->bnhde', kc, zeta, vc)
    decay = (gamma ** CHUNK)[None, :, None, None]

    def step(state, kv_n):
        return decay * state + kv_n, state

    _, r_prev = lax.scan(step, jnp.zeros((b, RET_HEADS, HEAD_DIM, HEAD_DIM), jnp.float32),
                         jnp.moveaxis(kv, 1, 0))
    r_prev = jnp.moveaxis(r_prev, 0, 1)
    cross = jnp.einsum('bnqhd,hq,bnhde->bnqhe', qc, xi, r_prev)
    y = rms_norm(inner + cross).reshape(b, s, RET_WIDTH)
    return (jax.nn.silu(g.astype(jnp.float32)) * y).astype(g.dtype)

def moe_ffn(h, router_w, router_b, w_gate, w_up, w_down):
    b, s, d = h.shape
    t = b * s
    hf = h.reshape(t, d)
    scores = jax.nn.sigmoid(jnp.dot(hf.astype(jnp.float32), router_w.astype(jnp.float32)))
    biased = (scores + router_b.astype(jnp.float32)).reshape(t, N_EXPERT_GROUPS, EXPERTS_PER_GROUP)
    group_score = lax.top_k(biased, 2)[0].sum(-1)
    _, g_idx = lax.top_k(group_score, 1)
    in_group = jnp.take_along_axis(biased, g_idx[:, :, None], axis=1)[:, 0]
    _, local = lax.top_k(in_group, TOP_K)
    e_idx = g_idx * EXPERTS_PER_GROUP + local
    gate_w = jnp.take_along_axis(scores, e_idx, axis=1)
    gate_w = gate_w / jnp.sum(gate_w, axis=-1, keepdims=True)
    flat_e = e_idx.reshape(-1)
    order = jnp.argsort(flat_e)
    tok = order // TOP_K
    sizes = jnp.bincount(flat_e, length=N_EXPERTS).astype(jnp.int32)
    xs = hf[tok]
    a = lax.ragged_dot(xs, w_gate, sizes)
    u = lax.ragged_dot(xs, w_up, sizes)
    ys = lax.ragged_dot(jax.nn.silu(a) * u, w_down, sizes)
    y = jnp.zeros_like(ys).at[order].set(ys).reshape(t, TOP_K, d)
    out = jnp.einsum('tkd,tk->td', y, gate_w.astype(y.dtype))
    return out.reshape(b, s, d)

def setup_inputs(seed: int = 0) -> dict:
    key = jax.random.key(seed)
    ks = jax.random.split(key, 16)
    f32 = jnp.float32
    n = lambda k, shape, sc: jax.random.normal(k, shape, f32) * sc
    return {
        "x": n(ks[0], (BATCH, SEQ, D_MODEL), 1.0),
        "norm_mix": 1.0 + n(ks[1], (DEPTH, D_MODEL), 0.1),
        "w_in": n(ks[2], (DEPTH, D_MODEL, D_IN), D_MODEL ** -0.5),
        "q_norm": 1.0 + n(ks[3], (DEPTH, HEAD_DIM), 0.1),
        "k_norm": 1.0 + n(ks[4], (DEPTH, HEAD_DIM), 0.1),
        "sinks": n(ks[5], (DEPTH, ATT_HEADS), 0.5),
        "pool_w": n(ks[6], (DEPTH, POOL_GROUPS, POOL_GROUP_DIM, POOL_GROUP_DIM), POOL_GROUP_DIM ** -0.5),
        "pool_scale": 1.0 + n(ks[7], (DEPTH, POOL_WIDTH), 0.1),
        "w_out": n(ks[8], (DEPTH, D_MIX, D_MODEL), 0.5 * D_MIX ** -0.5),
        "norm_ffn": 1.0 + n(ks[9], (DEPTH, D_MODEL), 0.1),
        "router_w": n(ks[10], (D_MODEL, N_EXPERTS), D_MODEL ** -0.5),
        "router_b": n(ks[11], (N_EXPERTS,), 0.01),
        "w_gate": n(ks[12], (DEPTH, N_EXPERTS, D_MODEL, D_EXPERT), D_MODEL ** -0.5),
        "w_up": n(ks[13], (DEPTH, N_EXPERTS, D_MODEL, D_EXPERT), D_MODEL ** -0.5),
        "w_down": n(ks[14], (DEPTH, N_EXPERTS, D_EXPERT, D_MODEL), 0.5 * D_EXPERT ** -0.5),
    }

def reference(x, norm_mix, w_in, q_norm, k_norm, sinks, pool_w, pool_scale, w_out,
              norm_ffn, router_w, router_b, w_gate, w_up, w_down):
    pos = jnp.arange(x.shape[1], dtype=jnp.float32)
    for l in range(DEPTH):
        h = rms_norm(x, norm_mix[l])
        proj = jnp.einsum('bsd,de->bse', h, w_in[l])
        q_a, k_a, v_a, u_b, q_c, k_c, v_c, g_c = jnp.split(proj, IN_SPLITS, axis=-1)
        y_a = sliding_window_sink_attention(q_a, k_a, v_a, q_norm[l], k_norm[l], sinks[l])
        y_b = multiscale_pool(u_b, pool_w[l], pool_scale[l])
        y_c = retention(q_c, k_c, v_c, g_c, pos)
        mix = jnp.concatenate([y_a, y_b, y_c], axis=-1)
        x = x + jnp.einsum('bse,ed->bsd', mix, w_out[l])
        x = x + moe_ffn(rms_norm(x, norm_ffn[l]), router_w, router_b, w_gate[l], w_up[l], w_down[l])
    return x


_drawn_inputs = setup_inputs


def setup_inputs(seed=0):
    import zlib

    import numpy as np

    out = dict(_drawn_inputs(seed))
    spreads = {}
    factors = {'sinks': 6.636}
    for name, (base, spread) in spreads.items():
        noise = np.random.default_rng([zlib.crc32(name.encode()), seed]).standard_normal(out[name].shape)
        drawn = base * np.exp(spread * noise) if base else spread * noise
        out[name] = __import__('jax').numpy.asarray(drawn.astype(out[name].dtype))
    for name, factor in factors.items():
        out[name] = (out[name] * factor).astype(out[name].dtype)
    return out
```

```python
from contextlib import ExitStack

import numpy as np

import concourse.bass as bass
from concourse import mybir

P = 128
SEQ, D, DEPTH = 2048, 1024, 2
TILES = SEQ // P
DC = D // P
DIN = 2048
HD = 64
QW, KVW, UW, RW = 512, 128, 256, 256
Q0, K0, V0 = 0, QW, QW + KVW
U0 = V0 + KVW
RQ0 = U0 + UW
RV0, RG0 = RQ0 + 2 * RW, RQ0 + 3 * RW
NE, DE = 32, 512
FC = DE // P
NT = 168
NT1 = NT - P
WIDTHS = (128, 136, 144, 152, NT)
ROUNDS = -(-SEQ // NT)
STRIDE = ROUNDS * NT
PADS = 256
EPS = 1e-6
BIG = 1e30
ARENA = 25024
WINDOWS = (2, 4, 8, 16)

F32 = mybir.dt.float32
I32 = mybir.dt.int32
U32 = mybir.dt.uint32
ALU = mybir.AluOpType
ACT = mybir.ActivationFunctionType
X = mybir.AxisListType.X

CONSTS = {}
_at = 0
for _name, _n in (("ident", P), ("before", P), ("ones", P), ("causal", P), ("pool_cur", 4 * P),
                  ("pool_first", 4 * P), ("pool_prev", 4 * P), ("gamma", 128), ("rev8", 8),
                  ("rev32", 32), ("slot0", 32), ("thr", ROUNDS), ("token", 1)):
    CONSTS[_name] = (_at, _n)
    _at += _n
NCONST = _at


def constant_arrays():
    c = np.zeros((P, NCONST), np.float64)

    def put(name, a):
        at, n = CONSTS[name]
        c[:, at:at + n] = np.asarray(a, np.float64).reshape(P, n)

    i, j = np.arange(P)[:, None], np.arange(P)[None, :]
    put("ident", i == j)
    put("before", i < j)
    put("ones", np.ones((P, P)))
    put("causal", i <= j)
    cur, first, prev = (np.zeros((P, 4, P)) for _ in range(3))
    for n, w in enumerate(WINDOWS):
        band = (j - i >= 0) & (j - i < w)
        cur[:, n] = band / w - (i == j)
        first[:, n] = band / np.minimum(j + 1, w) - (i == j)
        prev[:, n] = (j + P - i < w) / w
    put("pool_cur", cur)
    put("pool_first", first)
    put("pool_prev", prev)
    gamma = 1.0 - 2.0 ** (-5.0 - np.arange(4))
    g = np.zeros((2, 64, 2, 64))
    for h in range(4):
        g[h % 2, :, h // 2] = gamma[h] ** P
    put("gamma", g)
    put("rev8", np.tile(8 - np.arange(8), (P, 1)))
    put("rev32", np.tile(32 - np.arange(32), (P, 1)))
    put("slot0", np.tile(STRIDE * np.arange(NE), (P, 1)))
    put("thr", np.tile(NT * np.arange(ROUNDS), (P, 1)))
    put("token", i)

    freq = (1.0 / (10000.0 ** (np.arange(32) / 32.0)).astype(np.float32)).astype(np.float32)
    ang = (np.arange(SEQ, dtype=np.float32)[:, None] * freq[None, :]).astype(np.float64)
    at = (np.arange(SEQ) % P + 1)[:, None]
    scale = np.concatenate([gamma[None] ** at, gamma[None] ** -at * HD ** -0.5], 1)
    rot = np.stack([np.cos(ang), np.sin(ang)], 1)[:, :, None, :] * scale[:, None, :, None]

    pads = np.zeros((NE * STRIDE, 2), np.int32)
    pads[:, 0] = SEQ + np.arange(NE * STRIDE) % PADS
    return {"consts": c.astype(np.float32), "rot": rot.reshape(SEQ, 512).astype(np.float32),
            "pads": pads}


def small_parameters(norm_mix, norm_ffn, q_norm, k_norm, sinks, pool_w, pool_scale, router_w, router_b):
    both = lambda a: np.concatenate([a, a], 1)[:, :, None]
    per_chunk = lambda a: a.reshape(DEPTH, -1, P).transpose(0, 2, 1)
    heads = sinks.reshape(DEPTH, 2, 2, 2).transpose(0, 2, 3, 1)
    heads = np.broadcast_to(heads[:, :, None, :, :, None], (DEPTH, 2, 64, 2, 2, 2)).reshape(DEPTH, P, 8)
    maps = pool_w.reshape(DEPTH, 2, 2, 64, 64).transpose(0, 2, 3, 1, 4).reshape(DEPTH, P, P)
    router = np.broadcast_to(router_w.reshape(DC, P, NE).transpose(1, 0, 2).reshape(1, P, DC * NE), (DEPTH, P, DC * NE))
    bias = np.broadcast_to(router_b.reshape(1, 1, NE), (DEPTH, P, NE))
    return np.ascontiguousarray(np.concatenate(
        [per_chunk(norm_mix), per_chunk(norm_ffn), both(q_norm), both(k_norm), heads, maps,
         per_chunk(pool_scale), router, bias], 2))


def program(nc, x, small, w_in, w_out, w_gate, w_up, w_down, consts_d, rot_d, pads_d, out):
    hrows = nc.dram_tensor("hrows", (SEQ + PADS, D), F32).ap()
    table = nc.dram_tensor("table", (NE * STRIDE, 2), I32).ap()

    with ExitStack() as ctx:
        def sb(name, cols, dt=F32):
            return ctx.enter_context(nc.sbuf_tensor(name, [P, cols], dt))

        def sem(name):
            return ctx.enter_context(nc.semaphore(name))

        bank = [ctx.enter_context(nc.psum_tensor(f"bank{i}", [P, 512], F32)) for i in range(8)]
        bA, bB, bC, bD, bE, bF, bIP0, bIP1 = bank
        bIP = [bIP0, bIP1]

        cst = sb("cst", NCONST)

        def const(name, p0=0, p1=P):
            at, n = CONSTS[name]
            return cst[p0:p1, at:at + n]

        ident, before, ones, causal = (const(n) for n in ("ident", "before", "ones", "causal"))
        pool_cur = const("pool_cur").rearrange("p (g n) -> p g n", g=4)
        pool_first = const("pool_first").rearrange("p (g n) -> p g n", g=4)
        pool_prev = const("pool_prev").rearrange("p (g n) -> p g n", g=4)
        wts = sb("wts", 24576)
        win = wts[:, 0:16384].rearrange("p (n d c) -> p n d c", n=4, d=DC)
        wout = wts[:, 16384:24576].rearrange("p (d c) -> p d c", d=DC)
        wexp = wts[:, :].rearrange("p (b g n) -> p b g n", b=2, g=3)
        par = sb("par", 2 * DC + 2 + 8 + 128 + 2 + 256 + 32)
        gmix, gffn = par[:, 0:8], par[:, 8:16]
        qg, kg, sink = par[:, 16:17], par[:, 17:18], par[:, 18:26]
        pw = par[:, 26:154].rearrange("p (j e) -> p j e", j=2)
        pscale = par[:, 154:156]
        rw = par[:, 156:412].rearrange("p (d e) -> p d e", d=DC)
        rb = par[:, 412:444]
        qgs = sb("qgs", 1)
        base = sb("base", 32)
        count = sb("count", 4)
        rounds = sb("rounds", 1, I32)
        tab0 = sb("tab0", 64, I32)
        tab1 = sb("tab1", 64, I32)
        counts = sb("counts", 32, I32)
        cur = [sb(f"cur{b}", 4, I32) for b in range(2)]
        rows_in = [sb(f"rows_in{b}", 2, I32) for b in range(2)]
        stat = sb("stat", 64)
        newton = sb("newton", 48)
        tok = sb("tok", 2)

        arena = sb("arena", ARENA)
        used = {"mix": 0, "moe": 0}

        def part(phase, n):
            at = used[phase]
            used[phase] = at + n
            assert used[phase] <= ARENA, used
            return arena[:, at:at + n]

        xf = [part("mix", D) for _ in range(2)]
        xr = [part("mix", D) for _ in range(2)]
        hn, hT = part("mix", D), part("mix", D).rearrange("p (d n) -> p d n", d=DC)
        proj = [part("mix", DIN) for _ in range(2)]
        h2n, h2T = part("mix", D), part("mix", D).rearrange("p (d n) -> p d n", d=DC)
        sq, qn, kn = part("mix", 640), part("mix", 512), part("mix", 256)
        rk = part("mix", 512)
        rtmp = part("mix", 1024).rearrange("p (n h d) -> p n h d", n=4, h=8)
        rt = [part("mix", 512).rearrange("p (n h d) -> p n h d", n=2, h=8) for _ in range(2)]
        qT = part("mix", 512).rearrange("p (g c j n) -> p g c j n", g=2, c=2, j=2)
        kTr = part("mix", 512).rearrange("p (g c r n) -> p g c r n", g=2, c=2, r=2)
        rT = part("mix", 512).rearrange("p (j n) -> p j n", j=4)
        pr = part("mix", 1024).rearrange("p (a g n) -> p a g n", a=2, g=4)
        prT = part("mix", 1024).rearrange("p (a g n) -> p a g n", a=2, g=4)
        v0w = [part("mix", 128) for _ in range(2)]
        upv = [part("mix", 256) for _ in range(2)]
        iT = part("mix", 512).rearrange("p (h n) -> p h n", h=4)
        dT = part("mix", 256).rearrange("p (j n) -> p j n", j=2)
        state = [part("mix", 128).rearrange("p (j e) -> p j e", j=2) for _ in range(2)]
        kv = part("mix", 128).rearrange("p (j e) -> p j e", j=2)
        ysq, z = (part("mix", 256).rearrange("p (a j e) -> p a j e", a=2, j=2) for _ in range(2))
        yc = part("mix", 256)
        squares = part("mix", 512).bitcast(mybir.dt.bfloat16)
        eg, sg = part("mix", 256), part("mix", 256)
        mixT = part("mix", D).rearrange("p (d n) -> p d n", d=DC)
        es, sc, bi, mb, mb2 = (part("mix", 32) for _ in range(5))
        r32, oh1, oh2, pick, slots, junk = (part("mix", 32) for _ in range(6))
        g2, g2n = part("mix", 16).rearrange("p (g k) -> p g k", g=8), part("mix", 16).rearrange("p (g k) -> p g k", g=8)
        g8 = [part("mix", 8) for _ in range(6)]
        slotf = part("mix", 2)
        sloti = [sb(f"sloti{b}", 2, I32) for b in range(2)]
        pay = [sb(f"pay{b}", 4, I32) for b in range(2)]

        xg = part("moe", 2 * D).rearrange("p (k d) -> p k d", k=2)
        xT = part("moe", DC * NT).rearrange("p (d n) -> p d n", d=DC)
        sgm = part("moe", FC * NT).rearrange("p (f n) -> p f n", f=FC)
        hTm = part("moe", FC * NT).rearrange("p (f n) -> p f n", f=FC)
        yTs = part("moe", DC * NT).rearrange("p (d n) -> p d n", d=DC)
        ysb = part("moe", 2 * D).rearrange("p (k d) -> p k d", k=2)

        consts_full, pad_rows = sem("consts_full"), sem("pad_rows")
        par_full, wout_full = sem("par_full"), sem("wout_full")
        win_full = [sem(f"win_full{n}") for n in range(4)]
        xf_full, xr_full, rt_full = ([sem(f"{n}_full{b}") for b in range(2)] for n in ("xf", "xr", "rt"))
        x_stored, h_stored, table_clear = sem("x_stored"), sem("h_stored"), sem("table_clear")
        w_full = [[sem(f"w_full{g}{b}") for b in range(2)] for g in range(3)]
        tab_full = [sem(f"tab_full{b}") for b in range(2)]
        slots_written, gathered, added = sem("slots_written"), sem("gathered"), sem("added")
        sumsq_f, hn_ready, pe_hnT, hT_ready = sem("sumsq_f"), sem("hn_ready"), sem("pe_hnT"), sem("hT_ready")
        proj_psum, proj_ready = sem("proj_psum"), sem("proj_ready")
        qk_ready, rope_ready, pe_qkrT = sem("qk_ready"), sem("rope_ready"), sem("pe_qkrT")
        qkT_ready, rT_ready, pe_scores = sem("qkT_ready"), sem("rT_ready"), sem("pe_scores")
        neg_max, exp_done, probs_ready = sem("neg_max"), sem("exp_done"), sem("probs_ready")
        inner_ready, pe_h2T, h2T_ready, pe_router = sem("inner_ready"), sem("pe_h2T"), sem("h2T_ready"), sem("pe_router")
        pe_ykv, kvd_read, ysq_ready, z_ready = sem("pe_ykv"), sem("kvd_read"), sem("ysq_ready"), sem("z_ready")
        exp_gate, silu_ready, yc_ready = sem("exp_gate"), sem("silu_ready"), sem("yc_ready")
        pe_pT, pT_ready, pe_lin, pool_ready = sem("pe_pT"), sem("pT_ready"), sem("pe_lin"), sem("pool_ready")
        pe_ycT, ycT_ready, pe_pv, attn_ready = sem("pe_ycT"), sem("ycT_ready"), sem("pe_pv"), sem("attn_ready")
        vw_ready = sem("vw_ready")
        pe_oproj, x_new = sem("pe_oproj"), sem("x_new")
        sumsq_2, h2n_ready = sem("sumsq_2"), sem("h2n_ready")
        exp_router, picks_ready, pe_rank = sem("exp_router"), sem("picks_ready"), sem("pe_rank")
        rank_read = sem("rank_read")
        slots_ready = sem("slots_ready")
        passed = sem("passed")
        slots_free = sem("slots_free")
        rounds_ready = sem("rounds_ready")
        gu_done, down_done = sem("gu_done"), sem("down_done")
        pe_xT, xT_read = sem("pe_xT"), sem("xT_read")
        pe_y, y_read = sem("pe_y"), sem("y_read")
        silu_done, hid_ready, yT_ready = sem("silu_done"), sem("hid_ready"), sem("yT_ready")
        x_adds = sem("x_adds")
        targets_ready = sem("targets_ready")

        block = ctx.enter_context(nc.Block())

        def gu_at(f, k, w):
            n = 2 * f + k
            return (bC, bD, bE)[n // 3][:, (n % 3) * NT:(n % 3) * NT + w]

        def wait_alone(e, s, value):
            e.wait_ge(s, value)
            e.sem_inc(passed, 1)

        def steps(e, run):
            run(0, 0, True, False, False)
            run(1, 1, True, True, False)
            with e.Fori(0, (TILES - 4) // 2) as i:
                run(i * 2 + 2, 0, True, True, True)
                run(i * 2 + 3, 1, True, True, True)
            run(TILES - 2, 0, True, True, True)
            run(TILES - 1, 1, True, True, True)
            run(TILES, 0, False, True, True)
            run(TILES + 1, 1, False, False, True)

        def has_next(s):
            return not isinstance(s, int) or s < TILES - 1

        def experts(e, run):
            run(0, 0, 0)
            with e.Fori(0, NE // 2 - 1) as i:
                run(i * 2 + 1, i, 1)
                run(i * 2 + 2, i + 1, 0)
            run(NE - 1, NE // 2 - 1, 1)

        def half_count(l, s, b):
            if isinstance(s, int):
                return l * (TILES // 2 * 16) + (s // 2 + 1) * 16
            return l * (TILES // 2 * 16) + s * 8 + (16 if b == 0 else 8)

        def read_rounds(e, l):
            wait_alone(e, rounds_ready, l + 1)
            return e.value_load(rounds[0:1, 0:1], min_val=1, max_val=ROUNDS)

        def rows(t):
            return bass.ds(t * P, P)

        @block.sync
        def _(e):
            e.dma_start(cst[:, :], consts_d).then_inc(consts_full, 16)
            halves = e.alloc_register("sp_halves")
            e.reg_mov(halves, 0)

            with e.Fori(0, DEPTH) as l:
                h0 = e.snap(halves)
                def load_x(dst, full, t):
                    with e.If(l == 0):
                        e.dma_start(dst, x[rows(t), :]).then_inc(full, 16)
                    with e.Else():
                        e.dma_start(dst, out[rows(t), :]).then_inc(full, 16)

                def load_par():
                    e.dma_start(par[:, :], small[bass.ds(l, 1)].rearrange("o p n -> p (o n)")).then_inc(par_full, 16)

                with e.If(l == 0):
                    e.dma_start(xf[0], x[rows(0), :]).then_inc(xf_full[0], 16)
                    load_par()
                wait_alone(e, down_done, h0 * 2 + 1)
                for n in range(3):
                    e.dma_start(win[:, n], w_in[bass.ds(l, 1), :, n * 512:(n + 1) * 512].rearrange(
                        "o (d p) c -> p (o d) c", p=P)).then_inc(win_full[n], 16)
                wait_alone(e, down_done, h0 * 2 + 2)
                with e.If(l > 0):
                    load_par()
                    wait_alone(e, x_adds, h0 * 2 + 1)
                    e.dma_start(xf[0], out[rows(0), :]).then_inc(xf_full[0], 16)

                def rest():
                    e.dma_start(win[:, 3], w_in[bass.ds(l, 1), :, 1536:2048].rearrange(
                        "o (d p) c -> p (o d) c", p=P)).then_inc(win_full[3], 16)
                    e.dma_start(wout[:, :, :], w_out[bass.ds(l, 1)].rearrange(
                        "o (d p) c -> p (o d) c", p=P)).then_inc(wout_full, 16)
                    with e.If(l == 0):
                        wait_alone(e, x_adds, 1)
                        for k in range(PADS // P):
                            e.dma_start(hrows[SEQ + k * P:SEQ + (k + 1) * P, :], h2n).then_inc(pad_rows, 16)
                            e.dma_start(out[SEQ + k * P:SEQ + (k + 1) * P, :], h2n).then_inc(pad_rows, 16)
                    e.dma_start(table.rearrange("(p n) k -> p (n k)", p=P),
                                pads_d.rearrange("(p n) k -> p (n k)", p=P)).then_inc(table_clear, 16)

                def step(s, b, front, back, tail):
                    t0 = l * TILES + s
                    if tail:
                        wait_alone(e, h2n_ready, t0 - 1)
                        e.dma_start(hrows[rows(s - 2), :], h2n).then_inc(h_stored, 16)
                    if isinstance(s, int) and s == TILES:
                        wait_alone(e, proj_psum, (l + 1) * TILES * 4)
                        load_weights(0, 0)
                    if front:
                        if tail:
                            wait_alone(e, rope_ready, t0 - 1)
                        e.dma_start(rt[b].rearrange("p n h d -> p (n h d)"), rot_d[rows(s), :]).then_inc(rt_full[b], 16)
                        if back:
                            wait_alone(e, hn_ready, t0)
                        if has_next(s):
                            load_x(xf[1 - b], xf_full[1 - b], s + 1)
                        if tail:
                            wait_alone(e, x_stored, (t0 - 1) * 16)
                        load_x(xr[b], xr_full[b], s)
                    if front and not back:
                        rest()
                    if back:
                        wait_alone(e, x_new, t0 * 2)
                        e.dma_start(out[rows(s - 1), :], xr[1 - b]).then_inc(x_stored, 16)

                def load_weights(i, b, n=None):
                    for g in range(2):
                        for k, w in enumerate((w_gate, w_up)):
                            src = w[bass.ds(l, 1), bass.ds(i, 1), g * 512:(g + 1) * 512, :]
                            e.dma_start(wexp[:, b, g, k * 2048:(k + 1) * 2048].rearrange("p (d f) -> p d f", d=4),
                                        src.rearrange("o u (d p) f -> p (o u d) f", p=P)).then_inc(w_full[g][b], 16)
                    if n is not None:
                        wait_alone(e, down_done, n + 1)
                    for k in range(2):
                        src = w_down[bass.ds(l, 1), bass.ds(i, 1), k * 256:(k + 1) * 256, :]
                        e.dma_start(wexp[:, b, 2, k * 2048:(k + 1) * 2048].rearrange("p (f c) -> p f c", f=2),
                                    src.rearrange("o u (f p) c -> p (o u f) c", p=P)).then_inc(w_full[2][b], 16)

                steps(e, step)

                R = read_rounds(e, l)
                wait_alone(e, slots_written, (l + 1) * TILES * 32)
                with e.Fori(0, R) as r:
                    h = e.snap(halves)
                    wait_alone(e, x_adds, h * 2 + 1)

                    def expert(i, half, b):
                        n = h * 2 + i
                        slot = i * STRIDE + r * NT
                        wait_alone(e, gu_done, n * 2 + 2)
                        e.dma_start(tab0[:, :].rearrange("p (e k) -> p e k", k=2)[:, bass.ds(i, 1)].rearrange("p o k -> p (o k)"),
                                    table[bass.ds(slot, P), :]).then_inc(tab_full[b], 16)
                        e.dma_start(tab1[0:NT1, :].rearrange("p (e k) -> p e k", k=2)[:, bass.ds(i, 1)].rearrange("p o k -> p (o k)"),
                                    table[bass.ds(slot + P, NT1), :]).then_inc(tab_full[b], 16)
                        if isinstance(i, int) and i == 0:
                            with e.If(r > 0):
                                wait_alone(e, down_done, n + 1)
                                load_weights(i, b)
                            wait_alone(e, gathered, n * 32 + 32)
                        else:
                            load_weights(i, b, n)

                    experts(e, expert)
                    e.reg_add(halves, halves, NE // 2)
            wait_alone(e, x_adds, e.snap(halves) * 2 + 1)
            e.wait_ge(x_stored, DEPTH * TILES * 16)
            e.wait_ge(h_stored, DEPTH * TILES * 16)
            e.wait_ge(table_clear, DEPTH * 16)
            e.wait_ge(pad_rows, PADS // P * 32)

        @block.gpsimd
        def _(e):
            e.memset(h2n, 0.0)
            for k in range(2):
                e.memset(v0w[k], 0.0)
                e.memset(upv[k], 0.0)
            e.memset(kTr, 0.0)
            e.drain().then_inc(x_adds, 1)
            halves = e.alloc_register("pool_halves")
            e.reg_mov(halves, 0)

            with e.Fori(0, DEPTH) as l:
                def step(s, b, front, back, tail):
                    t0 = l * TILES + s
                    o = 1 - b
                    if back:
                        wait_alone(e, silu_ready, t0)
                        wait_alone(e, z_ready, t0)
                        e.tensor_tensor(yc.rearrange("p (j a e) -> p a j e", j=2, a=2), z,
                                        sg.rearrange("p (j a e) -> p a j e", j=2, a=2), ALU.mult).then_inc(yc_ready, 1)
                    if tail:
                        wait_alone(e, slots_ready, t0 - 1)
                        for k in range(2):
                            e.indirect_dma_start(
                                table, bass.IndirectOffsetOnAxis(ap=sloti[b][:, k:k + 1].bitcast(U32), axis=0),
                                pay[b][:, 2 * k:2 * k + 2], None).then_inc(slots_written, 16)
                    if front:
                        wait_alone(e, proj_ready, t0 * 4 + 3)
                        wait_alone(e, rt_full[b], half_count(l, s, b))
                        src = proj[b][:, RQ0:RQ0 + 512].rearrange("p (h k d) -> p h k d", h=8, k=2)
                        dst = rk.rearrange("p (h k d) -> p h k d", h=8, k=2)
                        cos, sin = rt[b][:, 0], rt[b][:, 1]
                        if back:
                            wait_alone(e, pe_ykv, t0)
                        e.tensor_tensor(rtmp[:, 0], src[:, :, 0], cos, ALU.mult)
                        e.tensor_tensor(rtmp[:, 1], src[:, :, 1], sin, ALU.mult)
                        e.tensor_tensor(rtmp[:, 2], src[:, :, 0], sin, ALU.mult)
                        e.tensor_tensor(rtmp[:, 3], src[:, :, 1], cos, ALU.mult)
                        e.drain()
                        e.tensor_tensor(dst[:, :, 0], rtmp[:, 0], rtmp[:, 1], ALU.subtract)
                        e.tensor_tensor(dst[:, :, 1], rtmp[:, 2], rtmp[:, 3], ALU.add)
                        e.drain()
                        e.tensor_copy(upv[b][96:128, :], proj[b][96:128, U0:U0 + UW]).then_inc(rope_ready, 1)
                        e.drain()
                        if back:
                            wait_alone(e, pe_pv, t0)
                        e.tensor_copy(v0w[b][0:64, :], proj[b][0:64, V0:V0 + KVW])
                        e.drain()
                        e.tensor_copy(v0w[o][64:128, :], proj[b][64:128, V0:V0 + KVW]).then_inc(vw_ready, 1)
                        e.drain()
                    if isinstance(s, int) and s == 1:
                        wait_alone(e, table_clear, (l + 1) * 16)
                    if tail:
                        wait_alone(e, slots_written, (t0 - 1) * 32)
                        e.nop().then_inc(slots_free, 1)

                steps(e, step)

                R = read_rounds(e, l)
                wait_alone(e, h_stored, (l + 1) * TILES * 16)
                wait_alone(e, x_stored, (l + 1) * TILES * 16)
                e.wait_ge(pad_rows, PADS // P * 32)
                with e.Fori(0, R):
                    h = e.snap(halves)

                    def slots_of(i, tab):
                        return tab.rearrange("p (e k) -> p e k", k=2)[:, bass.ds(i, 1)].rearrange("p o k -> p (o k)")

                    def gather(i, half, b):
                        wait_alone(e, tab_full[b], (h + half + 1) * 32)
                        e.tensor_copy(rows_in[b][:, 0:1], slots_of(i, tab0[:, :])[:, 0:1])
                        e.tensor_copy(rows_in[b][0:NT1, 1:2], slots_of(i, tab1[0:NT1, :])[:, 0:1])
                        e.drain()
                        e.indirect_dma_start(xg[:, 0, :], None, hrows, bass.IndirectOffsetOnAxis(
                            ap=rows_in[b][:, 0:1].bitcast(U32), axis=0)).then_inc(gathered, 16)
                        e.indirect_dma_start(xg[0:NT1, 1, :], None, hrows, bass.IndirectOffsetOnAxis(
                            ap=rows_in[b][0:NT1, 1:2].bitcast(U32), axis=0)).then_inc(gathered, 16)

                    def targets(i, b):
                        e.tensor_copy(cur[b][:, 0:2], slots_of(i, tab0[:, :]))
                        e.tensor_copy(cur[b][0:NT1, 2:4], slots_of(i, tab1[0:NT1, :]))

                    def add(n, b, following=None):
                        wait_alone(e, y_read, n * 4 + 1)
                        e.indirect_dma_start(out, bass.IndirectOffsetOnAxis(
                            ap=cur[b][:, 0:1].bitcast(U32), axis=0), ysb[:, 0, :], None,
                            compute_op=ALU.add).then_inc(added, 16)
                        e.indirect_dma_start(out, bass.IndirectOffsetOnAxis(
                            ap=cur[b][0:NT1, 2:3].bitcast(U32), axis=0), ysb[0:NT1, 1, :], None,
                            compute_op=ALU.add).then_inc(added, 16)
                        wait_alone(e, added, n * 32)
                        if following is not None:
                            targets(following, b)
                        e.drain().then_inc(x_adds, 1)

                    gather(0, 0, 0)
                    wait_alone(e, pe_xT, h * 8 + 4)
                    gather(1, 0, 1)
                    targets(0, 0)
                    targets(1, 1)
                    e.drain().then_inc(targets_ready, 1)
                    with e.Fori(0, NE // 2 - 1) as i:
                        wait_alone(e, pe_xT, (h * 2 + i * 2 + 2) * 4)
                        gather(i * 2 + 2, i + 1, 0)
                        add(h * 2 + i * 2 + 1, 0, i * 2 + 2)
                        wait_alone(e, pe_xT, (h * 2 + i * 2 + 3) * 4)
                        gather(i * 2 + 3, i + 1, 1)
                        add(h * 2 + i * 2 + 2, 1, i * 2 + 3)
                    add(h * 2 + NE - 1, 0)
                    add(h * 2 + NE, 1)
                    e.reg_add(halves, halves, NE // 2)

        @block.scalar
        def _(e):
            halves = e.alloc_register("act_halves")
            e.reg_mov(halves, 0)
            turns = e.alloc_register("act_turns")
            e.reg_mov(turns, 0)
            a = nc.scalar.activation

            with e.Fori(0, DEPTH) as l:
                e.wait_ge(par_full, (l + 1) * 16)

                def sumsq_front(s, b):
                    e.wait_ge(xf_full[b], half_count(l, s, b))
                    a(squares, xf[b], ACT.Square, accum_out=stat[:, 0:1]).then_inc(sumsq_f, 1)

                sumsq_front(0, 0)

                def step(s, b, front, back, tail):
                    t0 = l * TILES + s
                    o = 1 - b
                    if back:
                        e.wait_ge(pe_qkrT, t0)
                        for g in range(2):
                            a(qT[:, g].rearrange("p c j n -> p j c n"),
                              bC[:, 256 * g:256 * g + 256].rearrange("p (j c n) -> p j c n", j=2, c=2), ACT.Copy, scale=qgs[:, 0:1])
                        a(kTr[:, :, :, o], bD[:, 0:256].rearrange("p (g c n) -> p g c n", g=2, c=2), ACT.Copy,
                          scale=kg).then_inc(qkT_ready, 1)
                        e.wait_ge(proj_ready, t0 * 4)
                        a(eg, proj[o][:, RG0:RG0 + RW], ACT.Exp, scale=-1.0).then_inc(exp_gate, 1)
                    if front:
                        if has_next(s):
                            e.wait_ge(hn_ready, t0 + 1)
                            sumsq_front(s + 1, o)
                        e.wait_ge(proj_psum, t0 * 4 + 1)
                        a(proj[b][:, 0:512], bIP0[:, :], ACT.Copy).then_inc(proj_ready, 1)
                    if back:
                        e.wait_ge(neg_max, t0)
                        for k in range(2):
                            for g in range(4):
                                n = 4 * k + g
                                a(pr[:, k, g], (bC, bD)[k][:, g * P:(g + 1) * P], ACT.Exp, bias=stat[:, 16 + n:17 + n],
                                  scale=1.0, accum_out=stat[:, 24 + n:25 + n])
                        a(stat[:, 40:48], stat[:, 32:40], ACT.Exp).then_inc(exp_done, 1)
                    if front:
                        e.wait_ge(proj_psum, t0 * 4 + 2)
                        a(proj[b][:, 512:1024], bIP1[:, :], ACT.Copy).then_inc(proj_ready, 1)
                    if tail:
                        e.wait_ge(pe_router, t0 - 1)
                        a(es, bA[:, 0:32], ACT.Exp, scale=-1.0).then_inc(exp_router, 1)
                    if back:
                        e.wait_ge(pe_ykv, t0)
                        for k in range(2):
                            a(ysq[:, k], (bE, bF)[k][:, 0:128].rearrange("p (h e) -> p h e", h=2), ACT.Square)
                        e.drain().then_inc(ysq_ready, 1)
                    if front:
                        e.wait_ge(proj_psum, t0 * 4 + 3)
                        a(proj[b][:, 1024:1536], bIP0[:, :], ACT.Copy).then_inc(proj_ready, 1)
                    if back:
                        e.wait_ge(pe_pT, t0)
                        for k in range(2):
                            a(prT[:, k].rearrange("p g n -> p (g n)"), (bC, bD)[k][:, :], ACT.Copy)
                        e.drain().then_inc(pT_ready, 1)
                        e.wait_ge(pe_lin, t0)
                        for j in range(2):
                            a(mixT[:, 4 + j], bB[:, j * P:(j + 1) * P], ACT.Copy, scale=pscale[:, j:j + 1])
                        e.drain().then_inc(pool_ready, 1)
                    if front:
                        e.wait_ge(proj_psum, t0 * 4 + 4)
                        a(proj[b][:, 1536:2048], bIP1[:, :], ACT.Copy).then_inc(proj_ready, 1)
                    if back:
                        e.wait_ge(pe_pv, t0)
                        a(mixT[:, 0:4].rearrange("p j n -> p (j n)"), bF[:, :], ACT.Copy).then_inc(attn_ready, 1)
                        e.wait_ge(x_new, t0 * 2)
                        a(squares, xr[o], ACT.Square, accum_out=stat[:, 4:5]).then_inc(sumsq_2, 1)

                steps(e, step)

                R = read_rounds(e, l)
                with e.Fori(0, R):
                    h = e.snap(halves)

                    def y_out(n, b):
                        e.wait_ge(x_adds, n)
                        for k in range(4):
                            e.wait_ge(pe_y, (n - 1) * 4 + k + 1)
                            m = P if k < 2 else NT1
                            a(ysb[0:m, k // 2, (k % 2) * 512:(k % 2) * 512 + 512], (bA, bB)[k % 2][0:m, :],
                              ACT.Copy, scale=cur[b][0:m, 1 + 2 * (k // 2):2 + 2 * (k // 2)].bitcast(F32)).then_inc(y_read, 1)

                    def expert(i, half, b):
                        n = h * 2 + i
                        if isinstance(i, int) and i == 0:
                            e.wait_ge(targets_ready, e.snap(turns) + 1)
                        else:
                            y_out(n, 1 - b)
                        e.wait_ge(gu_done, n * 2 + 5)
                        a(sgm[:, 0:2], bC[:, 0:3 * NT].rearrange("p (k n) -> p k n", n=NT)[:, 0::2], ACT.Silu).then_inc(silu_done, 1)
                        a(sgm[:, 2], gu_at(2, 0, NT), ACT.Silu).then_inc(silu_done, 1)
                        e.wait_ge(gu_done, n * 2 + 6)
                        a(sgm[:, 3], gu_at(3, 0, NT), ACT.Silu).then_inc(silu_done, 1)
                        e.wait_ge(down_done, n + 3)
                        for k, bk in enumerate((bF, bIP0, bIP1)):
                            m = 3 if k < 2 else 2
                            a(yTs[:, 3 * k:3 * k + m].rearrange("p d n -> p (d n)"), bk[:, 0:m * NT], ACT.Copy)
                        e.drain().then_inc(yT_ready, 1)

                    experts(e, expert)
                    y_out(h * 2 + NE, 1)
                    e.reg_add(halves, halves, NE // 2)
                    e.reg_add(turns, turns, 1)

        @block.vector
        def _(e):
            v = nc.vector
            e.nop().then_inc(rank_read, 1)
            e.nop().then_inc(slots_free, 2)
            e.nop().then_inc(gu_done, 4)
            e.nop().then_inc(down_done, 2)
            e.nop().then_inc(y_read, 1)
            halves = e.alloc_register("dve_halves")
            e.reg_mov(halves, 0)

            def rstd(dst, src, n):
                w = dst.shape[1]
                val, y, t = newton[:, 0:w], newton[:, 16:16 + w], newton[:, 32:32 + w]
                v.tensor_scalar(val, src, 1.0 / n, EPS, ALU.mult, ALU.add)
                e.drain()
                v.tensor_scalar(t.bitcast(I32), val.bitcast(I32), 1, None, ALU.logical_shift_right)
                e.drain()
                v.tensor_scalar(y.bitcast(I32), t.bitcast(I32), -1.0, float(0x5f3759df), ALU.mult, ALU.add)
                e.drain()
                for k in range(3):
                    v.tensor_tensor(t, y, y, ALU.mult)
                    e.drain()
                    v.scalar_tensor_tensor(out=t, in0=t, scalar=-0.5, in1=val, op0=ALU.mult, op1=ALU.mult)
                    e.drain()
                    v.scalar_tensor_tensor(out=dst if k == 2 else y, in0=t, scalar=1.5, in1=y, op0=ALU.add, op1=ALU.mult)
                    e.drain()

            def bc(ap, shape):
                return ap.to_broadcast(shape)

            def norm_front(l, s):
                e.wait_ge(sumsq_f, l * TILES + s + 1)
                rstd(stat[:, 1:2], stat[:, 0:1], D)

            e.wait_ge(consts_full, 16)
            with e.Fori(0, DEPTH) as l:
                e.wait_ge(par_full, (l + 1) * 16)
                v.tensor_scalar(qgs[:, :], qg, HD ** -0.5, None, ALU.mult)
                v.tensor_copy(base[:, :], const("slot0"))
                v.memset(state[0], 0.0)
                e.drain()

                def hn_of(s, b):
                    norm_front(l, s)
                    v.tensor_scalar(hn, xf[b], stat[:, 1:2], None, ALU.mult).then_inc(hn_ready, 1)

                def hT_of(s):
                    e.wait_ge(pe_hnT, l * TILES + s + 1)
                    for k in range(2):
                        v.tensor_tensor(hT[:, 4 * k:4 * k + 4], (bA, bB)[k][:, :].rearrange("p (d n) -> p d n", d=4),
                                        bc(gmix[:, 4 * k:4 * k + 4].unsqueeze(2), [P, 4, P]), ALU.mult)
                    e.drain().then_inc(hT_ready, 1)

                e.wait_ge(x_adds, e.snap(halves) * 2 + 1)
                hn_of(0, 0)

                def step(s, b, front, back, tail):
                    t0 = l * TILES + s
                    o = 1 - b
                    if not (back or tail):
                        hT_of(s)
                    if back:
                        e.wait_ge(pe_qkrT, t0)
                        v.tensor_copy(rT.rearrange("p j n -> p (j n)"), bE[:, :]).then_inc(rT_ready, 1)
                    if back:
                        e.wait_ge(pe_scores, t0)
                        for k in range(2):
                            v.tensor_tensor(iT.rearrange("p (j a) n -> p a j n", a=2)[:, k],
                                            (bE, bF)[k][:, 0:256].rearrange("p (j n) -> p j n", j=2),
                                            bc(causal.unsqueeze(1), [P, 2, P]), ALU.mult)
                        e.drain().then_inc(inner_ready, 1)
                        if isinstance(s, int) and s == 1:
                            for k in range(2):
                                v.memset((bC, bD)[k][:, :].rearrange("p (g c n) -> p g c n", g=2, c=2)[:, :, 0, 64:128], -3e38)
                            e.drain()
                        for k in range(2):
                            v.tensor_reduce(stat[:, 8 + 4 * k:12 + 4 * k], (bC, bD)[k][:, :].rearrange("p (g n) -> p g n", g=4),
                                            X, ALU.max)
                        e.drain()
                        v.tensor_tensor(stat[:, 8:16], stat[:, 8:16], sink, ALU.max)
                        e.drain()
                        v.tensor_scalar(stat[:, 16:24], stat[:, 8:16], -1.0, None, ALU.mult)
                        v.tensor_tensor(stat[:, 32:40], sink, stat[:, 8:16], ALU.subtract)
                        e.drain().then_inc(neg_max, 1)
                    if tail:
                        e.wait_ge(pe_h2T, t0 - 1)
                        for k in range(2):
                            v.tensor_tensor(h2T[:, 4 * k:4 * k + 4], (bA, bB)[k][:, :].rearrange("p (d n) -> p d n", d=4),
                                            bc(gffn[:, 4 * k:4 * k + 4].unsqueeze(2), [P, 4, P]), ALU.mult)
                        e.drain().then_inc(h2T_ready, 1)
                    if back:
                        e.wait_ge(exp_gate, t0)
                        v.tensor_scalar(eg, eg, 1.0, None, ALU.add)
                        e.drain()
                        v.reciprocal(eg, eg)
                        e.drain()
                        v.tensor_tensor(sg, eg, proj[o][:, RG0:RG0 + RW], ALU.mult).then_inc(silu_ready, 1)
                        e.wait_ge(exp_done, t0)
                        v.tensor_tensor(stat[:, 24:32], stat[:, 24:32], stat[:, 40:48], ALU.add)
                        e.drain()
                        v.reciprocal(stat[:, 24:32], stat[:, 24:32])
                        e.drain()
                        v.tensor_tensor(pr.rearrange("p a g n -> p (a g) n"), pr.rearrange("p a g n -> p (a g) n"),
                                        bc(stat[:, 24:32].unsqueeze(2), [P, 8, P]), ALU.mult).then_inc(probs_ready, 1)
                        e.wait_ge(pe_ykv, t0)
                        v.tensor_tensor(kv, bB[:, 0:128].rearrange("p (j e) -> p j e", j=2), state[o], ALU.add)
                        v.tensor_copy(dT, bB[:, 256:512].rearrange("p (j n) -> p j n", j=2))
                        e.drain().then_inc(kvd_read, 1)
                        v.tensor_tensor(state[b], kv, const("gamma").rearrange("p (j e) -> p j e", j=2), ALU.mult)
                        e.wait_ge(ysq_ready, t0)
                        v.tensor_reduce(stat[:, 48:52], ysq.rearrange("p a j e -> p (a j) e"), X, ALU.add)
                        e.drain()
                        rstd(stat[:, 48:52], stat[:, 48:52], HD)
                        for k in range(2):
                            v.tensor_tensor(z[:, k], (bE, bF)[k][:, 0:128].rearrange("p (h e) -> p h e", h=2),
                                            bc(stat[:, 48 + 2 * k:50 + 2 * k].unsqueeze(2), [P, 2, HD]), ALU.mult)
                        e.drain().then_inc(z_ready, 1)
                    if tail:
                        route(l, s, b)
                    if back:
                        e.wait_ge(pe_ycT, t0)
                        v.tensor_copy(mixT[:, 6:8].rearrange("p j n -> p (j n)"), bE[:, 0:256]).then_inc(ycT_ready, 1)
                    if front:
                        e.wait_ge(proj_ready, t0 * 4 + 2)
                        v.tensor_tensor(sq, proj[b][:, 0:640], proj[b][:, 0:640], ALU.mult)
                        e.drain()
                        v.tensor_reduce(stat[:, 52:62], sq.rearrange("p (h d) -> p h d", h=10), X, ALU.add)
                        e.drain()
                        rstd(stat[:, 52:62], stat[:, 52:62], HD)
                        v.tensor_tensor(qn.rearrange("p (h d) -> p h d", h=8), proj[b][:, 0:512].rearrange("p (h d) -> p h d", h=8),
                                        bc(stat[:, 52:60].unsqueeze(2), [P, 8, HD]), ALU.mult)
                        for k in range(2):
                            v.tensor_tensor(kn.rearrange("p (g k d) -> p g k d", g=2, k=2)[:, :, k],
                                            proj[b][:, 512:640].rearrange("p (h d) -> p h d", h=2),
                                            bc(stat[:, 60:62].unsqueeze(2), [P, 2, HD]), ALU.mult)
                        e.drain().then_inc(qk_ready, 1)
                    if tail:
                        place(l, s, b)
                    if front and has_next(s):
                        hn_of(s + 1, o)
                        if not back:
                            hT_of(s + 1)
                    if back:
                        for k in range(2):
                            e.wait_ge(pe_oproj, (t0 - 1) * 2 + k + 1)
                            if k == 0:
                                e.wait_ge(xr_full[o], half_count(l, s - 1, o))
                            cols = slice(512 * k, 512 * k + 512)
                            v.tensor_tensor(xr[o][:, cols], xr[o][:, cols], bIP[k][:, :], ALU.add).then_inc(x_new, 1)
                            if k == 0 and front and has_next(s):
                                hT_of(s + 1)
                        e.wait_ge(sumsq_2, t0)
                        rstd(stat[:, 5:6], stat[:, 4:5], D)
                        if isinstance(s, int) and s == 1:
                            e.wait_ge(pad_rows, PADS // P * 32)
                        else:
                            e.wait_ge(h_stored, (t0 - 1) * 16)
                        v.tensor_scalar(h2n, xr[o], stat[:, 5:6], None, ALU.mult).then_inc(h2n_ready, 1)

                def first_of(vals, width, top, hot, rev):
                    v.tensor_reduce(top, vals, X, ALU.max)
                    e.drain()
                    v.scalar_tensor_tensor(out=r32[:, 0:width], in0=vals, scalar=top, in1=rev, op0=ALU.is_equal, op1=ALU.mult)
                    e.drain()
                    v.tensor_reduce(top, r32[:, 0:width], X, ALU.max)
                    e.drain()
                    v.tensor_scalar(hot, rev, top, None, ALU.is_equal)
                    e.drain()

                def route(l, s, b):
                    e.wait_ge(exp_router, l * TILES + s - 1)
                    v.tensor_scalar(es, es, 1.0, None, ALU.add)
                    e.drain()
                    v.reciprocal(sc, es)
                    e.drain()
                    v.tensor_tensor(bi, sc, rb, ALU.add)
                    e.drain()
                    b4 = bi.rearrange("p (g k j) -> p g k j", g=8, k=2)
                    v.tensor_tensor(g2, b4[:, :, :, 0], b4[:, :, :, 1], ALU.max)
                    v.tensor_tensor(g2n, b4[:, :, :, 0], b4[:, :, :, 1], ALU.min)
                    e.drain()
                    v.tensor_tensor(g8[0], g2[:, :, 0], g2[:, :, 1], ALU.max)
                    v.tensor_tensor(g8[1], g2[:, :, 0], g2[:, :, 1], ALU.min)
                    v.tensor_tensor(g8[2], g2n[:, :, 0], g2n[:, :, 1], ALU.max)
                    e.drain()
                    v.tensor_tensor(g8[1], g8[1], g8[2], ALU.max)
                    e.drain()
                    v.tensor_tensor(g8[0], g8[0], g8[1], ALU.add)
                    e.drain()
                    first_of(g8[0], 8, stat[:, 2:3], g8[3], const("rev8"))
                    v.tensor_scalar(g8[4], g8[3], 1.0, BIG, ALU.subtract, ALU.mult)
                    e.drain()
                    v.tensor_tensor(mb.rearrange("p (g k) -> p g k", g=8), bi.rearrange("p (g k) -> p g k", g=8),
                                    bc(g8[4].unsqueeze(2), [P, 8, 4]), ALU.add)
                    e.drain()
                    first_of(mb, 32, stat[:, 2:3], oh1, const("rev32"))
                    v.scalar_tensor_tensor(out=mb2, in0=oh1, scalar=-BIG, in1=mb, op0=ALU.mult, op1=ALU.add)
                    e.drain()
                    first_of(mb2, 32, stat[:, 2:3], oh2, const("rev32"))
                    v.tensor_tensor(pick, oh1, oh2, ALU.add).then_inc(picks_ready, 1)
                    v.tensor_tensor_reduce(junk, oh1, sc, 1.0, 0.0, ALU.mult, ALU.add, stat[:, 6:7])
                    e.drain()
                    v.tensor_tensor_reduce(junk, oh2, sc, 1.0, 0.0, ALU.mult, ALU.add, stat[:, 7:8])
                    e.drain()
                    v.tensor_tensor(stat[:, 3:4], stat[:, 6:7], stat[:, 7:8], ALU.add)
                    e.drain()
                    v.reciprocal(stat[:, 3:4], stat[:, 3:4])
                    e.drain()

                def place(l, s, b):
                    t0 = l * TILES + s
                    e.wait_ge(slots_free, t0 - 1)
                    v.tensor_scalar(pay[b][:, :].bitcast(F32).rearrange("p (k c) -> p k c", k=2)[:, :, 1], stat[:, 6:8],
                                    stat[:, 3:4], None, ALU.mult)
                    v.tensor_copy(pay[b][:, :].rearrange("p (k c) -> p k c", k=2)[:, :, 0], tok[:, :])
                    e.drain()
                    v.tensor_scalar(tok[:, :], tok[:, :], float(P), None, ALU.add)
                    e.wait_ge(pe_rank, t0 - 1)
                    v.tensor_tensor(slots, bA[:, 32:64], base[:, :], ALU.add)
                    e.drain()
                    v.tensor_tensor(base[:, :], bA[:, 64:96], base[:, :], ALU.add)
                    v.tensor_tensor_reduce(junk, oh1, slots, 1.0, 0.0, ALU.mult, ALU.add, slotf[:, 0:1])
                    e.drain()
                    v.tensor_tensor_reduce(junk, oh2, slots, 1.0, 0.0, ALU.mult, ALU.add, slotf[:, 1:2])
                    e.drain().then_inc(rank_read, 1)
                    v.tensor_copy(sloti[b][:, :], slotf).then_inc(slots_ready, 1)

                v.tensor_copy(tok[:, :], bc(const("token"), [P, 2]))
                e.drain()
                steps(e, step)

                v.tensor_tensor(base[:, :], base[:, :], const("slot0"), ALU.subtract)
                e.drain()
                v.tensor_copy(counts[:, :], base[:, :])
                v.tensor_reduce(count[:, 0:1], base[:, :], X, ALU.max)
                e.drain()
                v.tensor_scalar(junk[:, 0:ROUNDS], const("thr"), count[:, 0:1], None, ALU.is_lt)
                e.drain()
                v.tensor_reduce(count[:, 1:2], junk[:, 0:ROUNDS], X, ALU.add)
                e.drain()
                v.tensor_copy(rounds[:, :], count[:, 1:2]).then_inc(rounds_ready, 1)

                R = read_rounds(e, l)
                with e.Fori(0, R):
                    h = e.snap(halves)

                    def x_in(n):
                        for k in range(4):
                            e.wait_ge(pe_xT, n * 4 + k + 1)
                            v.tensor_tensor(xT[:, 2 * k:2 * k + 2], (bA, bB)[k % 2][:, 0:2 * NT].rearrange("p (d n) -> p d n", d=2),
                                            bc(gffn[:, 2 * k:2 * k + 2].unsqueeze(2), [P, 2, NT]), ALU.mult).then_inc(xT_read, 1)

                    x_in(h * 2)

                    def expert(i, half, b):
                        n = h * 2 + i
                        e.wait_ge(silu_done, n * 3 + 1)
                        v.tensor_tensor(hTm[:, 0], sgm[:, 0], gu_at(0, 1, NT), ALU.mult).then_inc(hid_ready, 1)
                        e.wait_ge(silu_done, n * 3 + 2)
                        v.tensor_tensor(hTm[:, 1:3], sgm[:, 1:3], bD[:, 0:3 * NT].rearrange("p (k n) -> p k n", n=NT)[:, 0::2],
                                        ALU.mult).then_inc(hid_ready, 1)
                        e.wait_ge(silu_done, n * 3 + 3)
                        v.tensor_tensor(hTm[:, 3], sgm[:, 3], gu_at(3, 1, NT), ALU.mult).then_inc(hid_ready, 1)
                        if not (isinstance(i, int) and i == NE - 1):
                            x_in(n + 1)

                    experts(e, expert)
                    e.reg_add(halves, halves, NE // 2)

        @block.tensor
        def _(e):
            tokens = e.alloc_register("pe_tokens")
            halves = e.alloc_register("pe_halves")
            e.reg_mov(halves, 0)
            mm = nc.tensor.matmul

            def tr(dst, src, m=P):
                return nc.tensor.transpose(dst, src, ident[0:m, 0:m])

            e.wait_ge(consts_full, 16)
            with e.Fori(0, DEPTH) as l:
                e.wait_ge(y_read, e.snap(halves) * 8 + 1)
                e.wait_ge(par_full, (l + 1) * 16)

                def step(s, b, front, back, tail):
                    t0 = l * TILES + s
                    o = 1 - b
                    first = isinstance(s, int) and s == 1

                    def chunk(n, part=(0, DC)):
                        if not front:
                            return
                        if part[0] == 0:
                            if n == 0:
                                e.wait_ge(hT_ready, t0 + 1)
                            e.wait_ge(win_full[n], (l + 1) * 16)
                            if n < 2 and tail:
                                e.wait_ge(x_new, (t0 - 2) * 2 + n + 1)
                            if n >= 2 or first:
                                e.wait_ge(proj_ready, t0 * 4 + n - 1)
                        for d in range(*part):
                            i = mm(bIP[n % 2][:, :], hT[:, d], win[:, n, d], start=(d == 0), stop=(d == DC - 1))
                        if part[1] == DC:
                            i.then_inc(proj_psum, 1)

                    def hn_transposes(t):
                        e.wait_ge(hn_ready, l * TILES + t + 1)
                        for d in range(DC):
                            i = tr((bA, bB)[d // 4][:, (d % 4) * P:(d % 4) * P + P], hn[:, d * P:(d + 1) * P])
                        i.then_inc(pe_hnT, 1)

                    if not (back or tail):
                        hn_transposes(s)
                    if not front:
                        e.wait_ge(rank_read, t0 - 1)
                        e.wait_ge(pool_ready, t0 - 1)
                    if back:
                        if not first:
                            e.wait_ge(pT_ready, t0 - 1)
                            e.wait_ge(ycT_ready, t0 - 1)
                        e.wait_ge(qk_ready, t0)
                        for j in range(4):
                            tr(bC[:, j * P:(j + 1) * P], qn[:, j * P:(j + 1) * P])
                        for g in range(2):
                            tr(bD[:, g * P:(g + 1) * P], kn[:, g * P:(g + 1) * P])
                        e.wait_ge(rope_ready, t0)
                        for j in range(4):
                            i = tr(bE[:, j * P:(j + 1) * P], rk[:, j * P:(j + 1) * P])
                        i.then_inc(pe_qkrT, 1)
                    chunk(0)
                    if back:
                        e.wait_ge(qkT_ready, t0)
                        for g in range(2):
                            for c in range(2):
                                for a in range(2):
                                    ph = slice(64 * a, 64 * a + 64)
                                    q = qT[ph, g, c].rearrange("p j n -> p (j n)")
                                    at = (2 * g + c) * P
                                    dst = (bC, bD)[a]
                                    if c == 0:
                                        f = kTr[ph, g].rearrange("p c r n -> p (c r) n")
                                        keys = f[:, o:4 - o:3 - 2 * o]
                                    else:
                                        keys = kTr[ph, g, :, o]
                                    mm(dst[:, at:at + P].rearrange("p (c n) -> p c n", c=2), q, keys, start=True, stop=True)
                        if not first:
                            e.wait_ge(attn_ready, t0 - 1)
                        e.wait_ge(rT_ready, t0)
                        for j in range(2):
                            for a in range(2):
                                ph = slice(64 * a, 64 * a + 64)
                                i = mm((bE, bF)[a][:, j * P:(j + 1) * P], rT[ph, 2 + j], rT[ph, j], start=True, stop=True)
                        i.then_inc(pe_scores, 1)
                    if tail:
                        e.wait_ge(h2n_ready, t0 - 1)
                        for d in range(DC):
                            i = tr((bA, bB)[d // 4][:, (d % 4) * P:(d % 4) * P + P], h2n[:, d * P:(d + 1) * P])
                        i.then_inc(pe_h2T, 1)
                    chunk(1)
                    if tail:
                        e.wait_ge(h2T_ready, t0 - 1)
                        for d in range(DC):
                            i = mm(bA[:, 0:32], h2T[:, d], rw[:, d], start=(d == 0), stop=(d == DC - 1))
                        i.then_inc(pe_router, 1)
                    if back:
                        u = proj[o][:, U0:U0 + UW]
                        rv = proj[o][:, RV0:RV0 + RW]
                        for h in range(4):
                            ph = slice(64 * (h % 2), 64 * (h % 2) + 64)
                            mm(bB[ph, 64 * (h // 2):64 * (h // 2) + 64], rk[:, 256 + 64 * h:320 + 64 * h],
                               rv[:, 64 * h:64 * h + 64], start=True, stop=True)
                        for g in range(4):
                            ph = slice(64 * (g % 2), 64 * (g % 2) + 64)
                            dst = bB[ph, 256 + P * (g // 2):256 + P * (g // 2) + P]
                            uc = u[:, 64 * g:64 * g + 64]
                            if first:
                                mm(dst, uc, pool_first[:, g], start=True, stop=True)
                            else:
                                mm(dst, uc, pool_cur[:, g], start=True, stop=False)
                                mm(dst, upv[b][96:128, 64 * g:64 * g + 64], pool_prev[96:128, g], start=False, stop=True)
                        e.wait_ge(inner_ready, t0)
                        if not first:
                            e.wait_ge(z_ready, t0 - 1)
                        for a in range(2):
                            for j in range(2):
                                ph = slice(64 * a, 64 * a + 64)
                                dst = (bE, bF)[a][:, 64 * j:64 * j + 64]
                                hh = 2 * j + a
                                mm(dst, rT[ph, j], state[o][ph, j], start=True, stop=False)
                                i = mm(dst, iT[:, hh], rv[:, 64 * hh:64 * hh + 64], start=False, stop=True)
                        i.then_inc(pe_ykv, 1)
                    chunk(2)
                    if back:
                        e.wait_ge(probs_ready, t0)
                        for a in range(2):
                            for g in range(4):
                                i = tr((bC, bD)[a][:, g * P:(g + 1) * P], pr[:, a, g])
                        i.then_inc(pe_pT, 1)
                        wait_alone(e, kvd_read, t0)
                        for g in range(4):
                            ph = slice(64 * (g % 2), 64 * (g % 2) + 64)
                            i = mm(bB[ph, P * (g // 2):P * (g // 2) + P], pw[ph, g // 2], dT[ph, g // 2], start=True, stop=True)
                        i.then_inc(pe_lin, 1)
                        e.wait_ge(yc_ready, t0)
                        for j in range(2):
                            i = tr(bE[:, j * P:(j + 1) * P], yc[:, j * P:(j + 1) * P])
                        i.then_inc(pe_ycT, 1)
                    chunk(3, (0, 4))
                    if back:
                        e.wait_ge(pT_ready, t0)
                        e.wait_ge(vw_ready, t0)
                        for a in range(2):
                            ph = slice(64 * a, 64 * a + 64)
                            for g in range(2):
                                for c in range(2):
                                    val = (v0w[o] if c == 0 else proj[o][:, V0:V0 + KVW])[:, 64 * g:64 * g + 64]
                                    dst = bF[ph, :].rearrange("p (j n) -> p j n", j=4)[:, 2 * g:2 * g + 2, 64 * c:64 * c + 64]
                                    i = mm(dst, val, prT[:, a, 2 * g + c], start=True, stop=True)
                        i.then_inc(pe_pv, 1)
                    if tail:
                        e.wait_ge(picks_ready, t0 - 1)
                        mm(bA[:, 32:64], before, pick, start=True, stop=True)
                        mm(bA[:, 64:96], ones, pick, start=True, stop=True).then_inc(pe_rank, 1)
                    chunk(3, (4, DC))
                    if back:
                        e.wait_ge(wout_full, (l + 1) * 16)
                        e.wait_ge(pool_ready, t0)
                        e.wait_ge(ycT_ready, t0)
                        for k in range(2):
                            if front:
                                e.wait_ge(proj_ready, t0 * 4 + 3 + k)
                            elif k == 0:
                                e.wait_ge(x_new, (t0 - 2) * 2 + 2)
                            for n, d in enumerate((4, 5, 6, 7, 0, 1, 2, 3)):
                                if n == 4 and k == 0:
                                    e.wait_ge(attn_ready, t0)
                                i = mm(bIP[k][:, :], mixT[:, d], wout[:, d, 512 * k:512 * k + 512], start=(n == 0), stop=(n == DC - 1))
                            i.then_inc(pe_oproj, 1)
                            if k == 0 and front and has_next(s):
                                if tail:
                                    e.wait_ge(rank_read, t0)
                                hn_transposes(s + 1)
                    elif front:
                        hn_transposes(s + 1)

                steps(e, step)

                R = read_rounds(e, l)
                e.wait_ge(x_new, (l + 1) * TILES * 2)
                wait_alone(e, rank_read, (l + 1) * TILES + 1)
                with e.Fori(0, R) as r:
                    h = e.snap(halves)
                    seen = e.snap(r * NT)

                    def x_in(n, first, ks=range(4)):
                        if ks[0] == 0:
                            e.wait_ge(gathered, (n + 1) * 32)
                        for k in ks:
                            if k < 2 and not first:
                                e.wait_ge(y_read, (n - 1) * 4 + k)
                            if k >= 2:
                                e.wait_ge(xT_read, n * 4 + k - 1)
                            for j in range(2):
                                d = 2 * k + j
                                at = (bA, bB)[k % 2][:, j * NT:j * NT + NT]
                                tr(at[:, 0:P], xg[:, 0, d * P:(d + 1) * P])
                                i = tr(at[:, P:NT], xg[0:NT1, 1, d * P:(d + 1) * P], NT1)
                            i.then_inc(pe_xT, 1)

                    def y_out(n, ks=range(4)):
                        if ks[0] == 0:
                            e.wait_ge(yT_ready, n)
                        for k in ks:
                            if k >= 2:
                                wait_alone(e, y_read, (n - 1) * 4 + k)
                            m0, m = (0, P) if k < 2 else (P, NT1)
                            for j in range(4):
                                d = 4 * (k % 2) + j
                                i = tr((bA, bB)[k % 2][0:m, j * P:(j + 1) * P], yTs[:, d, m0:m0 + m])
                            i.then_inc(pe_y, 1)

                    def hidden(b, f, k, d, w):
                        lhs = wexp[:, b, d // 4, k * 2048 + d % 4 * 512 + f * P:k * 2048 + d % 4 * 512 + f * P + P]
                        start = d == 0 and k == 0 and f != 1
                        return mm(gu_at(f, k, w), lhs, xT[:, d, 0:w], start=start, stop=(d == DC - 1), skip_group_check=True)

                    e.wait_ge(y_read, h * 8 + 1)
                    x_in(h * 2, True)

                    def products(i, n, half, b, w):
                        first, last = (isinstance(i, int) and i == k for k in (0, NE - 1))
                        for d in range(4):
                            for k in range(2):
                                for f in range(FC):
                                    hidden(b, f, k, d, w)
                            if d == 0 and not last:
                                e.reg_load(tokens, counts[0:1, bass.ds(i + 1, 1)])
                            if not first and d >= 1:
                                y_out(n, ((0, 1), (2,), (3,))[d - 1])
                        wait_alone(e, w_full[1][b], (h + half + 1) * 32)
                        for f in range(FC):
                            for k in range(2):
                                for d in range(4, DC):
                                    j = hidden(b, f, k, d, w)
                            if f >= 2:
                                j.then_inc(gu_done, 1)
                        if not last:
                            x_in(n + 1, isinstance(i, int), (0, 1))
                        wait_alone(e, w_full[2][b], (h + half + 1) * 32)
                        for f in range(FC):
                            if f != 2:
                                wait_alone(e, hid_ready, n * 3 + (1, 2, 2, 3)[f])
                            for d in range(DC):
                                lhs = wexp[:, b, 2, f * D + d * P:f * D + d * P + P]
                                dst = (bF, bIP0, bIP1)[d // 3][:, (d % 3) * NT:(d % 3) * NT + w]
                                j = mm(dst, lhs, hTm[:, f, 0:w], start=(f == 0 and d % 3 == 0), stop=(f == FC - 1), skip_group_check=True)
                            if f < 2 and not last:
                                x_in(n + 1, False, (f + 2,))
                        j.then_inc(down_done, 1)

                    def expert(i, half, b):
                        n = h * 2 + i

                        def at_width(k0, k1):
                            if k1 - k0 == 1:
                                products(i, n, half, b, WIDTHS[k0])
                                return
                            k = (k0 + k1) // 2
                            with e.If(e.snap(tokens) <= seen + WIDTHS[k - 1]):
                                at_width(k0, k)
                            with e.Else():
                                at_width(k, k1)

                        e.wait_ge(xT_read, n * 4 + 4)
                        wait_alone(e, w_full[0][b], (h + half + 1) * 32)
                        if isinstance(i, int) and i == 0:
                            products(i, n, half, b, NT)
                        else:
                            at_width(0, len(WIDTHS))

                    experts(e, expert)
                    y_out(h * 2 + NE)
                    e.reg_add(halves, halves, NE // 2)


_SMALL = ["norm_mix", "norm_ffn", "q_norm", "k_norm", "sinks", "pool_w", "pool_scale", "router_w", "router_b"]


def kernel(**inputs):
    import concourse.bacc as bacc
    from concourse.bass_utils import run_bass_kernel_spmd

    nc = bacc.Bacc("TRN2", target_bir_lowering=False, num_devices=1)
    inputs = {name: np.ascontiguousarray(a) for name, a in inputs.items()}
    arrays = {"x": inputs["x"].reshape(SEQ, D), "small": small_parameters(*(inputs[n] for n in _SMALL))}
    arrays.update((name, inputs[name]) for name in ("w_in", "w_out", "w_gate", "w_up", "w_down"))
    arrays.update(constant_arrays())
    arrays = {f"in_{name}": a for name, a in arrays.items()}
    args = [nc.dram_tensor(name, a.shape, mybir.dt.from_np(a.dtype), kind="ExternalInput").ap()
            for name, a in arrays.items()]
    out = nc.dram_tensor("out", (SEQ + PADS, D), F32, kind="ExternalOutput").ap()
    program(nc, *args, out)
    r = run_bass_kernel_spmd(nc, [arrays], core_ids=[0]).results[0]["out"]
    return r[:SEQ].reshape(1, SEQ, D)
```
